# Optimizing a Trainium2 kernel written in Bass

```python
import math
import jax, jax.numpy as jnp
from jax import lax
import numpy as np

D_MODEL = 2048
BATCH = 1
SEQ = 256
DEPTH = 2

N_A_LAYERS = DEPTH // 2
N_B_LAYERS = DEPTH - N_A_LAYERS

SSM_EXPAND = 2
D_INNER = SSM_EXPAND * D_MODEL
SSM_HEADDIM = 64
N_SSM_HEADS = D_INNER // SSM_HEADDIM
N_SSM_GROUPS = 8
HEADS_PER_GROUP = N_SSM_HEADS // N_SSM_GROUPS
D_STATE = 128
CONV_W = 4
SSD_CHUNK = 128
GN = N_SSM_GROUPS * D_STATE
CONV_DIM = D_INNER + 2 * GN
D_IN_PROJ = D_INNER + CONV_DIM + N_SSM_HEADS

HEAD_DIM = 64
N_Q_HEADS = D_MODEL // HEAD_DIM
N_KV_HEADS = 8
Q_PER_KV = N_Q_HEADS // N_KV_HEADS
WINDOW = 128
KV_WIDTH = N_KV_HEADS * HEAD_DIM
ROPE_THETA = 10000.0
ATTN_SCALE = 1.0 / math.sqrt(HEAD_DIM)

D_FF = 4 * D_MODEL

DEEPNORM_ALPHA = (2.0 * DEPTH) ** 0.25
DEEPNORM_BETA = (8.0 * DEPTH) ** -0.25

LN_EPS = 1e-5
RMS_EPS = 1e-5

kernel_name = 'yoco_ssd_swa_sink_hybrid'

def _layernorm(x, g, b):
    xf = x.astype(jnp.float32)
    mu = jnp.mean(xf, axis=-1, keepdims=True)
    var = jnp.mean(jnp.square(xf - mu), axis=-1, keepdims=True)
    y = (xf - mu) * lax.rsqrt(var + LN_EPS) * g.astype(jnp.float32) + b.astype(jnp.float32)
    return y.astype(x.dtype)

def _ssd_chunked_scan(xs, dt, A, Bm, Cm):
    bsz, length = xs.shape[0], xs.shape[1]
    n_chunks = length // SSD_CHUNK

    def to_chunks(t):
        return jnp.moveaxis(t.reshape(bsz, n_chunks, SSD_CHUNK, *t.shape[2:]), 1, 0)

    xdt = xs.astype(jnp.float32) * dt[..., None]
    dA = dt * A
    causal = jnp.tril(jnp.ones((SSD_CHUNK, SSD_CHUNK), dtype=bool))

    def step(state, inp):
        xdt_c, dA_c, b_c, c_c = inp
        cs = jnp.cumsum(dA_c, axis=1)
        seg = cs[:, :, None] - cs[:, None, :]
        decay = jnp.exp(jnp.where(causal[None, :, :, None, None], seg, -jnp.inf))
        cb = jnp.einsum('bign,bjgn->bgij', c_c, b_c)
        y_intra = jnp.einsum('bgij,bijgh,bjghp->bighp', cb, decay, xdt_c)
        y_inter = jnp.einsum('bign,bghpn->bighp', c_c, state) * jnp.exp(cs)[..., None]
        to_end = jnp.exp(cs[:, -1:] - cs)
        new_state = (state * jnp.exp(cs[:, -1])[..., None, None]
                     + jnp.einsum('bjgn,bjgh,bjghp->bghpn', b_c, to_end, xdt_c))
        return new_state, y_intra + y_inter

    state0 = jnp.zeros((bsz, N_SSM_GROUPS, HEADS_PER_GROUP, SSM_HEADDIM, D_STATE), jnp.float32)
    _, y = lax.scan(step, state0, (to_chunks(xdt), to_chunks(dA),
                                   to_chunks(Bm.astype(jnp.float32)),
                                   to_chunks(Cm.astype(jnp.float32))))
    return jnp.moveaxis(y, 0, 1).reshape(bsz, length, N_SSM_GROUPS, HEADS_PER_GROUP, SSM_HEADDIM)

def _mamba2_mixer(h, w_in, conv_w, conv_b, dt_bias, A_log, D_skip, norm_w, w_out):
    bsz, length, _ = h.shape
    zxbcdt = h @ w_in
    z = zxbcdt[..., :D_INNER]
    xbc = zxbcdt[..., D_INNER:D_INNER + CONV_DIM]
    dt_raw = zxbcdt[..., D_INNER + CONV_DIM:]
    xbc = lax.conv_general_dilated(
        xbc, conv_w[:, None, :].astype(xbc.dtype), window_strides=(1,),
        padding=[(CONV_W - 1, 0)], dimension_numbers=('NWC', 'WIO', 'NWC'),
        feature_group_count=CONV_DIM)
    xbc = jax.nn.silu(xbc + conv_b)
    xs = xbc[..., :D_INNER].reshape(bsz, length, N_SSM_GROUPS, HEADS_PER_GROUP, SSM_HEADDIM)
    Bm = xbc[..., D_INNER:D_INNER + GN].reshape(bsz, length, N_SSM_GROUPS, D_STATE)
    Cm = xbc[..., D_INNER + GN:].reshape(bsz, length, N_SSM_GROUPS, D_STATE)
    dt = jax.nn.softplus(dt_raw.astype(jnp.float32) + dt_bias.astype(jnp.float32))
    dt = dt.reshape(bsz, length, N_SSM_GROUPS, HEADS_PER_GROUP)
    A = -jnp.exp(A_log.astype(jnp.float32)).reshape(N_SSM_GROUPS, HEADS_PER_GROUP)
    y = _ssd_chunked_scan(xs, dt, A, Bm, Cm)
    y = y + D_skip.astype(jnp.float32).reshape(N_SSM_GROUPS, HEADS_PER_GROUP)[..., None] * xs.astype(jnp.float32)
    y = y.reshape(bsz, length, D_INNER) * jax.nn.silu(z.astype(jnp.float32))
    yg = y.reshape(bsz, length, N_SSM_GROUPS, D_INNER // N_SSM_GROUPS)
    yg = yg * lax.rsqrt(jnp.mean(jnp.square(yg), axis=-1, keepdims=True) + RMS_EPS)
    y = yg.reshape(bsz, length, D_INNER) * norm_w.astype(jnp.float32)
    return y.astype(h.dtype) @ w_out

def _rope_tables(length):
    inv_freq = ROPE_THETA ** (-jnp.arange(0, HEAD_DIM, 2, dtype=jnp.float32) / HEAD_DIM)
    ang = jnp.arange(length, dtype=jnp.float32)[:, None] * inv_freq[None, :]
    return jnp.cos(ang), jnp.sin(ang)

def _rope(t, cos, sin):
    tf = t.astype(jnp.float32)
    t1, t2 = tf[..., :HEAD_DIM // 2], tf[..., HEAD_DIM // 2:]
    c, s = cos[None, :, None, :], sin[None, :, None, :]
    return jnp.concatenate([t1 * c - t2 * s, t2 * c + t1 * s], axis=-1).astype(t.dtype)

def _shared_kv(h, kv_w, cos, sin):
    bsz, length, _ = h.shape
    kv = h @ kv_w
    k = kv[..., :KV_WIDTH].reshape(bsz, length, N_KV_HEADS, HEAD_DIM)
    v = kv[..., KV_WIDTH:].reshape(bsz, length, N_KV_HEADS, HEAD_DIM)
    return _rope(k, cos, sin), v

def _swa_sink_attention(h, w_q, sinks, w_o, k, v, cos, sin):
    bsz, length, _ = h.shape
    n_blocks = length // WINDOW
    q = _rope((h @ w_q).reshape(bsz, length, N_Q_HEADS, HEAD_DIM), cos, sin)
    qb = jnp.moveaxis(q.reshape(bsz, n_blocks, WINDOW, N_KV_HEADS, Q_PER_KV, HEAD_DIM), 1, 0)

    def band(t):
        tp = jnp.pad(t, ((0, 0), (WINDOW, 0), (0, 0), (0, 0)))
        prev = tp[:, :length].reshape(bsz, n_blocks, WINDOW, N_KV_HEADS, HEAD_DIM)
        cur = t.reshape(bsz, n_blocks, WINDOW, N_KV_HEADS, HEAD_DIM)
        return jnp.moveaxis(jnp.concatenate([prev, cur], axis=2), 1, 0)

    kb, vb = band(k), band(v)
    qi = jnp.arange(WINDOW)[:, None]
    kc = jnp.arange(2 * WINDOW)[None, :]
    dist = qi + WINDOW - kc
    in_band = (dist >= 0) & (dist < WINDOW)
    sink = sinks.astype(jnp.float32).reshape(N_KV_HEADS, Q_PER_KV)[None, :, :, None, None]

    def one_block(args):
        q_blk, k_blk, v_blk, blk_idx = args
        s = jnp.einsum('bqkgd,bckd->bkgqc', q_blk, k_blk).astype(jnp.float32) * ATTN_SCALE
        valid = in_band & ((blk_idx > 0) | (kc >= WINDOW))
        s = jnp.where(valid, s, -jnp.inf)
        m = jnp.maximum(jnp.max(s, axis=-1, keepdims=True), sink)
        p = jnp.exp(s - m)
        w = p / (jnp.sum(p, axis=-1, keepdims=True) + jnp.exp(sink - m))
        return jnp.einsum('bkgqc,bckd->bqkgd', w.astype(v_blk.dtype), v_blk)

    o = lax.map(one_block, (qb, kb, vb, jnp.arange(n_blocks)))
    o = jnp.moveaxis(o, 0, 1).reshape(bsz, length, N_Q_HEADS * HEAD_DIM)
    return o @ w_o

def _sqrelu_mlp(h, w1, w2):
    return jnp.square(jax.nn.relu(h @ w1)) @ w2

def setup_inputs(seed: int = 0) -> dict:
    key = jax.random.key(seed)
    ks = jax.random.split(key, 20)
    f32 = jnp.float32
    nrm = lambda k, shape, scale: jax.random.normal(k, shape, f32) * scale
    x = jax.random.normal(ks[0], (BATCH, SEQ, D_MODEL), f32)
    a_w_in = nrm(ks[1], (N_A_LAYERS, D_MODEL, D_IN_PROJ), D_MODEL ** -0.5)
    a_conv_w = nrm(ks[2], (N_A_LAYERS, CONV_W, CONV_DIM), CONV_W ** -0.5)
    a_conv_b = nrm(ks[3], (N_A_LAYERS, CONV_DIM), 0.02)
    dt0 = jnp.exp(jax.random.uniform(ks[4], (N_A_LAYERS, N_SSM_HEADS), f32,
                                     math.log(1e-3), math.log(1e-1)))
    a_dt_bias = dt0 + jnp.log(-jnp.expm1(-dt0))
    a_A_log = jnp.log(jax.random.uniform(ks[5], (N_A_LAYERS, N_SSM_HEADS), f32, 1.0, 16.0))
    a_D = 1.0 + nrm(ks[6], (N_A_LAYERS, N_SSM_HEADS), 0.1)
    a_norm_w = 1.0 + nrm(ks[7], (N_A_LAYERS, D_INNER), 0.02)
    a_w_out = nrm(ks[8], (N_A_LAYERS, D_INNER, D_MODEL), DEEPNORM_BETA * D_INNER ** -0.5)
    kv_w = jnp.concatenate([
        nrm(ks[9], (D_MODEL, KV_WIDTH), D_MODEL ** -0.5),
        nrm(ks[10], (D_MODEL, KV_WIDTH), DEEPNORM_BETA * D_MODEL ** -0.5)], axis=1)
    b_w_q = nrm(ks[11], (N_B_LAYERS, D_MODEL, N_Q_HEADS * HEAD_DIM), D_MODEL ** -0.5)
    b_sinks = nrm(ks[12], (N_B_LAYERS, N_Q_HEADS), 0.5)
    b_w_o = nrm(ks[13], (N_B_LAYERS, N_Q_HEADS * HEAD_DIM, D_MODEL),
                DEEPNORM_BETA * (N_Q_HEADS * HEAD_DIM) ** -0.5)
    mlp_w1 = nrm(ks[14], (DEPTH, D_MODEL, D_FF), DEEPNORM_BETA * D_MODEL ** -0.5)
    mlp_w2 = nrm(ks[15], (DEPTH, D_FF, D_MODEL), DEEPNORM_BETA * D_FF ** -0.5)
    ln_g = 1.0 + nrm(ks[16], (DEPTH, 2, D_MODEL), 0.02)
    ln_b = nrm(ks[17], (DEPTH, 2, D_MODEL), 0.02)
    return {'x': x, 'a_w_in': a_w_in, 'a_conv_w': a_conv_w, 'a_conv_b': a_conv_b,
            'a_dt_bias': a_dt_bias, 'a_A_log': a_A_log, 'a_D': a_D, 'a_norm_w': a_norm_w,
            'a_w_out': a_w_out, 'kv_w': kv_w, 'b_w_q': b_w_q, 'b_sinks': b_sinks,
            'b_w_o': b_w_o, 'mlp_w1': mlp_w1, 'mlp_w2': mlp_w2, 'ln_g': ln_g, 'ln_b': ln_b}

def reference(x, a_w_in, a_conv_w, a_conv_b, a_dt_bias, a_A_log, a_D, a_norm_w, a_w_out,
              kv_w, b_w_q, b_sinks, b_w_o, mlp_w1, mlp_w2, ln_g, ln_b):
    length = x.shape[1]
    cos, sin = _rope_tables(length)
    h = x
    k_shared, v_shared = None, None
    for layer in range(DEPTH):
        if layer < N_A_LAYERS:
            mix = _mamba2_mixer(h, a_w_in[layer], a_conv_w[layer], a_conv_b[layer],
                                a_dt_bias[layer], a_A_log[layer], a_D[layer],
                                a_norm_w[layer], a_w_out[layer])
        else:
            if layer == N_A_LAYERS:
                k_shared, v_shared = _shared_kv(h, kv_w, cos, sin)
            j = layer - N_A_LAYERS
            mix = _swa_sink_attention(h, b_w_q[j], b_sinks[j], b_w_o[j],
                                      k_shared, v_shared, cos, sin)
        h = _layernorm(DEEPNORM_ALPHA * h + mix, ln_g[layer, 0], ln_b[layer, 0])
        h = _layernorm(DEEPNORM_ALPHA * h + _sqrelu_mlp(h, mlp_w1[layer], mlp_w2[layer]),
                       ln_g[layer, 1], ln_b[layer, 1])
    return h


_drawn_inputs = setup_inputs


def setup_inputs(seed=0):
    import zlib

    import numpy as np

    out = dict(_drawn_inputs(seed))
    spreads = {}
    factors = {'a_conv_b': 6.149, 'a_norm_w': 23.728, 'b_sinks': 29.712}
    for name, (base, spread) in spreads.items():
        noise = np.random.default_rng([zlib.crc32(name.encode()), seed]).standard_normal(out[name].shape)
        drawn = base * np.exp(spread * noise) if base else spread * noise
        out[name] = __import__('jax').numpy.asarray(drawn.astype(out[name].dtype))
    for name, factor in factors.items():
        out[name] = (out[name] * factor).astype(out[name].dtype)
    return out
```

```python
from collections import defaultdict
from contextlib import contextmanager

import numpy as np

import concourse.bass as bass
from concourse import mybir

F32 = mybir.dt.float32
F32R = mybir.dt.float32r
ACT = mybir.ActivationFunctionType
ALU = mybir.AluOpType
AX = mybir.AxisListType

P = 128
T = 256
NH = T // P
D = 2048
KT = D // P
DI = 4096
NG = 8
GH = 8
HD = 64
GW = GH * HD
DS = 128
NHD = NG * GH
FF = 8192
KV = 8
QB = 4
WIN = 128
BLK = 512
ALPHA = float((2.0 * 2) ** 0.25)
EPS = 1e-5
SCALE = HD ** -0.5
NEG = -1.0e30
COL_Z, COL_XS, COL_B, COL_C, COL_DT = 0, DI, 2 * DI, 2 * DI + NG * DS, 2 * DI + 2 * NG * DS

CH = 1024
RAW = 4
RING = 8
LEAD = 6
GROUP_CHUNKS = 20
SLAB_CHUNKS = 32

K_ID, K_TRI, K_STRI, K_SMASK, K_AMASK, K_SEL, K_COS, K_SIN, K_END = 0, 128, 256, 384, 512, 768, 832, 896, 960


OUTPUT_PIECES = [(h, slice(c, c + D // 2)) for h in range(NH) for c in (0, D // 2)]


class Counts:

    def __init__(self, eng, by_dma):
        self.eng, self.by_dma = eng, by_dma
        self.n = defaultdict(int)
        self.base = defaultdict(int)

    def step(self, sem):
        return 16 if sem in self.by_dma else 1

    def up(self, sem):
        self.n[sem] += 1
        return self.step(sem)

    def now(self, sem, back=0):
        return (self.base[sem] + (self.n[sem] - back)) * self.step(sem)

    def next(self, sem, k=1):
        self.n[sem] += k
        return self.now(sem)

    def any(self, sem, back=0):
        return not isinstance(self.base[sem], int) or self.n[sem] > back

    @contextmanager
    def loop(self, times, before, times_of):
        start = dict(self.n)
        per = {sem: times_of * (n - before.get(sem, 0)) for sem, n in start.items()}
        with self.eng.Fori(0, times) as i:
            for sem, k in per.items():
                if k:
                    self.base[sem] = i * k
            yield i
        for sem, n in self.n.items():
            assert n - start.get(sem, 0) == per.get(sem, 0), (sem, n - start.get(sem, 0), per.get(sem, 0))
        for sem, k in per.items():
            self.base[sem] = 0
            self.n[sem] = start[sem] + k * times


def build(nc, t, out):
    w_hi_done = nc.alloc_semaphore("w_hi_done")
    w_split = nc.alloc_semaphore("w_split")
    w_used = nc.alloc_semaphore("w_used")
    act_hi_done = nc.alloc_semaphore("act_hi_done")
    act_split = nc.alloc_semaphore("act_split")
    o_split = nc.alloc_semaphore("o_split")
    cross_out = nc.alloc_semaphore("cross_out")
    dve_step = nc.alloc_semaphore("dve_step")
    pool_step = nc.alloc_semaphore("pool_step")
    selection_ready = nc.alloc_semaphore("selection_ready")
    heads_selected = nc.alloc_semaphore("heads_selected")
    nab_ready = nc.alloc_semaphore("nab_ready")
    uexp_ready = nc.alloc_semaphore("uexp_ready")
    dt_ready = nc.alloc_semaphore("dt_ready")
    cs_ready = nc.alloc_semaphore("cs_ready")
    cs_split = nc.alloc_semaphore("cs_split")
    conv_done = nc.alloc_semaphore("conv_done")
    tanh_done = nc.alloc_semaphore("tanh_done")
    xT_ready = nc.alloc_semaphore("xT_ready")
    z_tanh_done = nc.alloc_semaphore("z_tanh_done")
    xdt_ready = nc.alloc_semaphore("xdt_ready")
    m_ready = nc.alloc_semaphore("m_ready")
    y_ready = nc.alloc_semaphore("y_ready")
    y_squared = nc.alloc_semaphore("y_squared")
    rstd_ready = nc.alloc_semaphore("rstd_ready")
    y_normed = nc.alloc_semaphore("y_normed")
    yT_done = nc.alloc_semaphore("yT_done")
    mean_var_ready = nc.alloc_semaphore("mean_var_ready")
    h0_normed = nc.alloc_semaphore("h0_normed")
    h1_normed = nc.alloc_semaphore("h1_normed")
    h0_affine = nc.alloc_semaphore("h0_affine")
    h1_affine = nc.alloc_semaphore("h1_affine")
    centred = nc.alloc_semaphore("centred")
    res_ready = nc.alloc_semaphore("res_ready")
    f_squared = nc.alloc_semaphore("f_squared")
    k_turned = nc.alloc_semaphore("k_turned")
    q_turned = nc.alloc_semaphore("q_turned")
    maxima_ready = nc.alloc_semaphore("maxima_ready")
    exps_ready = nc.alloc_semaphore("exps_ready")
    full = [nc.alloc_semaphore(f"full{b}") for b in range(8)]
    free = [nc.alloc_semaphore(f"free{b}") for b in range(8)]
    output_ready = nc.alloc_semaphore("output_ready")
    loaded = [nc.alloc_semaphore(f"loaded{s}") for s in range(RAW)]
    consts_in = nc.alloc_semaphore("consts_in")
    vectors_in = nc.alloc_semaphore("vectors_in")
    per_head_in = nc.alloc_semaphore("per_head_in")
    x_in = nc.alloc_semaphore("x_in")
    x_again_in = nc.alloc_semaphore("x_again_in")
    gains_in = nc.alloc_semaphore("gains_in")
    out_done = nc.alloc_semaphore("out_done")
    by_dma = {*loaded, consts_in, vectors_in, per_head_in, x_in, x_again_in, gains_in, out_done}

    at = [(nc.sbuf_base + 31) // 32 * 32]

    def place(name, shape, dt=F32, offset=None):
        size = int(np.prod(shape[1:])) * 4
        if offset is None:
            offset = at[0]
            at[0] += (size + 31) // 32 * 32
        return nc.alloc_sbuf_tensor_at(name, shape, dt, offset=offset)

    raw = place("raw", [P, RAW, CH])
    whi = place("whi", [P, RING, CH], F32R)
    wlo = place("wlo", [P, RING, CH], F32R)
    actA = place("actA", [P, KT, 2, T], F32R)
    y_at = at[0]
    actB = place("actB", [P, KT, 2, T], F32R)
    yT = place("yT", [P, DI // P, T], F32, y_at)
    res_at = at[0]
    res = place("res", [P, NH, D])
    ident = place("ident", [P, P])
    ident_r = place("ident_r", [P, P], F32R)
    smask_r = place("smask_r", [P, P], F32R)
    amask_r = place("amask_r", [P, 2, P], F32R)
    cs2 = place("cs2", [P, NH, P], F32R)
    ncs2 = place("ncs2", [P, NH, P], F32R)
    sel2 = place("sel2", [P, NHD])
    sel_at = at[0]
    sel8 = place("sel8", [P, GH, P], F32R)
    cw = place("cw", [P, NG * 6 * 5])
    cwg = place("cwg", [P, 2, 30])
    nw = place("nw", [P, DI // P])
    lng = place("lng", [P, 4, KT])
    lnb = place("lnb", [P, 4, KT])
    dt = place("dt", [P, NH, NHD])
    te = place("te", [P, NHD])
    ecs = place("ecs", [P, NHD])
    Dsk = place("Dsk", [P, NHD])
    cosb = place("cosb", [P, NH, 32])
    sinb = place("sinb", [P, NH, 32])
    sink = place("sink", [P, 32])
    small = place("small", [P, 112])
    scr = (at[0] + 31) // 32 * 32
    space = nc.sbuf_usable_end - scr

    def region(start, limit):
        pos = [start]

        def put(name, shape, dtype=F32):
            x = place(name, shape, dtype, pos[0])
            pos[0] += (int(np.prod(shape[1:])) * 4 + 31) // 32 * 32
            assert pos[0] <= limit, (name, pos[0] - limit)
            return x
        return put

    end = nc.sbuf_usable_end
    put = region(res_at, res_at + NH * D * 4)
    em = put("em", [P, NH, GH * P])
    xdt = put("xdt", [P, NH, GW])
    xD = put("xD", [P, NH, GW])
    xin = place("xin", [P, NH, D], F32, res_at)
    put = region(scr, end)
    xT = put("xT", [P, 2, 6, T])
    xpad = put("xpad", [P, 2, 3 + T + 1])
    crossb = put("crossb", [P, 2, T])
    xh = put("xh", [P, 2, T])
    thb = put("thb", [P, 2, T])
    yb = put("yb", [P, NH, GW])
    zs = put("zs", [P, NH, GW])
    xde = put("xde", [P, GW])
    bcb = put("bcb", [P, 3, P])
    st = put("st", [P, GW])
    put = region(y_at, y_at + KT * 2 * T * 4)
    kst = put("kst", [P, K_END])
    vst = put("vst", [P, 5, P])
    nst = put("nst", [P, P])
    gst = put("gst", [P, 2, P])
    dtb = put("dtb", [P, NHD])
    alg = put("alg", [P, NHD])
    eA = put("eA", [P, NHD])
    dv = put("dv", [P, 12, NH * NHD])
    csr = place("csr", [P, NH, NHD], F32R, y_at + 24 * 1024)
    cshl = place("cshl", [P, NH, 2, NHD], F32, y_at + 25 * 1024)
    assert y_at + 24 * 1024 > y_at + 4 * (K_END + 5 * P + P + 2 * P + 3 * NHD + 12 * P)
    act1 = place("act1", [P, KT, 2, T], F32R, scr)
    gb = place("gb", [P, 2, D], F32, scr)
    put = region(scr + 2 * D * 4, end)
    mcross = put("mcross", [P, 2, T])
    fb = put("fb", [P, 2, T])
    fsq = put("fsq", [P, 2, T])
    hf = put("hf", [P, 2, BLK])
    put = region(scr + 2 * D * 4, end)
    ropeA = put("ropeA", [P, BLK])
    ropeB = put("ropeB", [P, BLK])
    qtok = put("qtok", [P, NH, BLK])
    kz = put("kz", [P, KV, T])
    vtok = place("vtok", [P, NH, BLK], F32, sel_at)
    otok = put("otok", [P, BLK])
    put = region(scr, scr + 2 * D * 4)
    pb = put("pb", [P, 4, T])
    pT = put("pT", [P, 8, P])
    qT = put("qT", [P, 4, T])

    ps = nc.alloc_psum_tensor("ps", [P, 8, BLK], F32)

    ss, var, rstd, nrt = small[:, 0:2], small[:, 2:4], small[:, 4:6], small[:, 6:8]
    mhalf, per_gw, epsilon, three_half, minus_one, nmr = [small[:, k:k + 2] for k in (8, 96, 98, 100, 102, 104)]
    mvb = small[:, 10:14].rearrange("p (c k) -> p c k", c=2)
    bst = small[:, 16:64].rearrange("p (c k) -> p c k", c=2)
    mx, mm_, nm, sb_, es, rs, den, rinv = [small[:, 64 + 4 * i:68 + 4 * i] for i in range(8)]

    def column_chunk(w, r, c, n=BLK):
        rows = CH // n * P
        return w[bass.ds(r, rows), bass.ds(c, n)].rearrange("(k p) n -> p k n", p=P)

    def group_chunks(g):
        cols = [COL_B + g * DS, COL_C + g * DS] + [COL_XS + g * GW + i * P for i in range(4)]
        for c in cols:
            for r in range(2):
                yield t["w_in"], r * CH, c, P
        for r in range(8):
            yield t["w_in"], r * 2 * P, COL_Z + g * GW, BLK

    def slab_chunks(w, row):
        for nb in range(4):
            for r in range(8):
                yield w, row + r * 2 * P, nb * BLK, BLK

    def mlp_chunks(layer, s):
        for i in range(16):
            for r in range(2):
                yield t["w1"][layer], r * CH, s * D + i * P, P
        yield from slab_chunks(t["w2"][layer], s * D)

    block = nc.Block()
    with block:

        @block.sync
        def _(e):
            C = Counts(e, by_dma)
            n = [0]

            def load(w, r, c, cols, also_next=False, wait=True):
                if wait and C.any(w_split, back=-1 if also_next else 0):
                    e.wait_ge(w_split, C.now(w_split, back=-1 if also_next else 0))
                C.n[w_split] += 1
                s = n[0] % RAW
                e.dma_start(
                    raw[:, s, :].rearrange("p (k n) -> p k n", n=cols), column_chunk(w, r, c, cols)).then_inc(
                        loaded[s], C.up(loaded[s]))
                n[0] += 1

            def load_group(g):
                for k, args in enumerate(group_chunks(g)):
                    load(*args, also_next=(k == 11), wait=(k != 12))

            C.n[w_split] = 1 - RAW
            e.dma_start(kst[:, :], t["consts"]).then_inc(consts_in, 16)
            load(t["w_in"], 0, COL_DT, NHD)
            for g in range(2):
                before = dict(C.n)
                load_group(g)
            with C.loop(3, before, 2) as i:
                for b in range(2):
                    load_group(2 * i + 2 + b)
            for half in range(2):
                for args in slab_chunks(t["w_out"], half * D):
                    load(*args)

            def mlp(layer):
                before = dict(C.n)
                for args in mlp_chunks(layer, 0):
                    load(*args)
                with C.loop(2, before, 1) as i:
                    for args in mlp_chunks(layer, i + 1):
                        load(*args)
                for args in mlp_chunks(layer, 3):
                    load(*args)

            mlp(0)
            for w, blocks in ((t["kv_w"], 2), (t["w_q"], QB)):
                for nb in range(blocks):
                    for r in range(8):
                        load(w, r * 2 * P, nb * BLK, BLK)
            for args in slab_chunks(t["w_o"], 0):
                load(*args)
            mlp(1)
            for h, cols in OUTPUT_PIECES:
                e.wait_ge(output_ready, C.next(output_ready))
                e.dma_start(out[0, h * P:(h + 1) * P, cols], res[:, h, cols]).then_inc(out_done, C.up(out_done))
            e.wait_ge(out_done, C.now(out_done))

        @block.tensor
        def _(e):
            C = Counts(e, by_dma)

            def emptied(b):
                if C.any(free[b]):
                    e.wait_ge(free[b], C.now(free[b]))

            def fill(b, counted=True):
                emptied(b)
                C.n[free[b]] += counted

            def chunk():
                s = C.n[w_split] % RING
                e.wait_ge(w_split, C.next(w_split))
                return s

            def row_tile(b, act, ready=()):
                if 0 in ready:
                    e.wait_ge(act_split, C.next(act_split, 2))
                fill(b)
                for h in range(2):
                    s = chunk()
                    for k in range(8):
                        kt = 8 * h + k
                        if kt and kt in ready:
                            e.wait_ge(act_split, C.next(act_split, 2))
                        w = slice(k * P, (k + 1) * P)
                        e.matmul(ps[:, b, :].rearrange("p (a n) -> p a n", a=2), whi[:, s, w], act[:, kt, :, :],
                                 start=(kt == 0), stop=False)
                        last = e.matmul(ps[:, b, T:2 * T], wlo[:, s, w], act[:, kt, 0, :],
                                        start=False, stop=(kt == KT - 1))
                    last.then_inc(w_used, C.up(w_used))

            def column_chunk_products(b0, act, c, ready=0):
                if ready:
                    e.wait_ge(act_split, C.next(act_split, ready))
                s = chunk()
                for k in range(2):
                    kt = 2 * c + k
                    w = slice(k * BLK, (k + 1) * BLK)
                    for h in range(NH):
                        tk = slice(h * P, (h + 1) * P)
                        e.matmul(ps[:, b0 + h, :], act[:, kt, 0, tk], whi[:, s, w], start=(kt == 0), stop=False)
                        e.matmul(ps[:, b0 + h, :], act[:, kt, 0, tk], wlo[:, s, w], start=False, stop=False)
                        last = e.matmul(ps[:, b0 + h, :], act[:, kt, 1, tk], whi[:, s, w], start=False,
                                        stop=(kt == KT - 1))
                last.then_inc(w_used, C.up(w_used))

            def column_block(b0, act, ready=None, after=None):
                if (ready or {}).get(0, 0) == 4:
                    e.wait_ge(act_split, C.next(act_split, 4))
                    ready = {4: 4}
                fill(b0)
                fill(b0 + 1)
                for c in range(8):
                    column_chunk_products(b0, act, c, (ready or {}).get(c, 0))
                    for f in (after or {}).get(c, ()):
                        f()

            def slab(act, ready=None, after=None):
                for nb in range(4):
                    column_block(2 * (nb % 2), act, ready if nb == 0 else None, after if nb == 0 else None)

            def transposes(b, tiles, counted=True):
                fill(b, counted)
                for i, x in enumerate(tiles):
                    last = e.transpose(ps[:, b, i * P:(i + 1) * P], x, ident[:, :])
                last.then_inc(full[b], C.up(full[b]))

            e.wait_ge(consts_in, C.next(consts_in))
            e.wait_ge(vectors_in, C.next(vectors_in, 6))
            fill(0)
            e.wait_ge(dve_step, C.next(dve_step))
            for k in range(5):
                last = e.transpose(ps[:, 0, k * 48:(k + 1) * 48], vst[0:48, k, :], ident[0:48, 0:48])
            last = e.transpose(ps[:, 0, 240:272], nst[0:32, :], ident[0:32, 0:32])
            last.then_inc(full[0], C.up(full[0]))
            fill(1)
            for k in range(2):
                last = e.transpose(ps[:, 1, k * 64:(k + 1) * 64], gst[0:64, k, :], ident[0:64, 0:64])
            last.then_inc(full[1], C.up(full[1]))
            e.wait_ge(x_in, C.next(x_in, 2))
            for g in range(4):
                for h in range(NH):
                    transposes((2 + 2 * g + h) % 8, [xin[:, h, (4 * g + i) * P:(4 * g + i + 1) * P] for i in range(4)],
                               counted=False)

            s = chunk()
            e.wait_ge(act_split, C.next(act_split, 2))
            for h in range(NH):
                fill(2 + h)
            for kt in range(KT):
                if kt % 4 == 0 and kt:
                    e.wait_ge(act_split, C.next(act_split, 2))
                for h in range(NH):
                    tk = slice(h * P, (h + 1) * P)
                    w = slice(kt * NHD, (kt + 1) * NHD)
                    o = ps[:, 2 + h, 0:NHD]
                    e.matmul(o, actA[:, kt, 0, tk], whi[:, s, w], start=(kt == 0), stop=False)
                    e.matmul(o, actA[:, kt, 0, tk], wlo[:, s, w], start=False, stop=False)
                    last = e.matmul(o, actA[:, kt, 1, tk], whi[:, s, w], start=False, stop=(kt == KT - 1))
            last.then_inc(w_used, C.up(w_used))

            def dt_sums():
                e.wait_ge(dt_ready, C.next(dt_ready))
                fill(4)
                for c in range(NH):
                    last = e.matmul(ps[:, 4, c * NHD:(c + 1) * NHD], kst[:, K_TRI:K_TRI + P],
                                    dv[:, 11, c * NHD:(c + 1) * NHD], start=True, stop=True)
                last.then_inc(full[4], C.up(full[4]))
                fill(5)
                e.matmul(ps[:, 5, 0:NHD], kst[:, K_STRI:K_STRI + P], dv[:, 11, 0:NHD],
                                       start=True, stop=True).then_inc(full[5], C.up(full[5]))

            def cs_transposes():
                e.wait_ge(cs_split, C.next(cs_split))
                transposes(6, [cshl[:, c, :, :].rearrange("p a n -> p (a n)") for c in range(NH)])

            def s1(par):
                e.wait_ge(xT_ready, C.now(xT_ready))
                for c in range(NH):
                    transposes(4 + c, [xT[:, par, 2 + i, c * P:(c + 1) * P] for i in range(4)])
                fill(6)
                e.transpose(ps[:, 6, 0:P], xT[:, par, 0, 0:P], ident[:, :])
                for c in range(NH):
                    tk = slice(c * P, (c + 1) * P)
                    last = e.matmul(ps[:, 6, (1 + c) * P:(2 + c) * P], xT[:, par, 0, tk], xT[:, par, 1, tk],
                                    start=True, stop=True)
                last.then_inc(full[6], C.up(full[6]))

            def seg(c, hh, b):
                fill(b)
                o = ps[:, b, :].rearrange("p (h n) -> p h n", h=4)
                e.matmul(o, ident_r[:, :], smask_r[:, :].unsqueeze(1).broadcast_to([P, 4, P]), start=True, stop=False)
                e.matmul(o, ncs2[:, c, :], sel8[:, 4 * hh:4 * hh + 4, :], start=False, stop=False)
                for h in range(4):
                    last = e.matmul(ps[:, b, h * P:(h + 1) * P], sel8[:, 4 * hh + h, :], cs2[:, c, :],
                                    start=False, stop=(h == 3))
                last.then_inc(full[b], C.up(full[b]))

            def s2():
                e.wait_ge(heads_selected, C.next(heads_selected))
                seg(0, 0, 7)
                seg(0, 1, 6)

            def s3():
                seg(1, 0, 7)
                seg(1, 1, 6)

            def intra(c, b):
                e.wait_ge(m_ready, C.next(m_ready))
                fill(b)
                for h in range(GH):
                    last = e.matmul(ps[:, b, h * HD:(h + 1) * HD], em[:, c, h * P:(h + 1) * P],
                                    xdt[:, c, h * HD:(h + 1) * HD], start=True, stop=True)
                last.then_inc(full[b], C.up(full[b]))

            def s4():
                e.wait_ge(xdt_ready, C.next(xdt_ready))
                fill(4)
                e.matmul(ps[:, 4, :], bcb[:, 0, :], xde[:, :], start=True, stop=True).then_inc(full[4], C.up(full[4]))
                intra(0, 5)

            def s5(par):
                intra(1, 7)
                emptied(4)
                fill(6)
                e.matmul(ps[:, 6, :], xT[:, par, 1, P:T], st[:, :], start=True, stop=True).then_inc(
                    full[6], C.up(full[6]))

            def s67():
                for c in range(NH):
                    e.wait_ge(y_normed, C.next(y_normed))
                    transposes(4 + c, [xdt[:, c, i * P:(i + 1) * P] for i in range(4)])

            def group(par, prev=None, first=False):
                pieces = {}
                if prev is not None:
                    pieces = {0: lambda: s1(prev), 1: s2, 2: s3, 3: s4, 4: lambda: s5(prev)}
                if first:
                    pieces = {0: dt_sums, 2: cs_transposes}
                for i in range(6):
                    row_tile(i % 2, actA)
                    if i in pieces:
                        pieces[i]()
                    if i == 0:
                        C.n[xT_ready] += 6
                column_block(2, actA, after={5: [s67]} if prev is not None else None)

            group(0, first=True)
            before = dict(C.n)
            group(1, 0)
            with C.loop(3, before, 2):
                group(0, 1)
                group(1, 0)

            s1(1)
            slab(actA, ready={0: 1, 2: 1, 4: 1, 6: 1},
                 after={0: [s2], 1: [s3], 3: [s4], 5: [lambda: s5(1)], 7: [s67]})
            slab(act1, ready={0: 1, 2: 1, 4: 1, 6: 1})

            def norm_transposes():
                for g in range(4):
                    for h in range(NH):
                        normed = (h0_normed, h1_normed)[h]
                        e.wait_ge(normed, C.next(normed))
                        transposes(g + 4 * (1 - h), [res[:, h, (4 * g + i) * P:(4 * g + i + 1) * P] for i in range(4)],
                                   counted=False)

            def mlp_slab(first):
                for i in range(16):
                    row_tile(4 + i % 2, actA, ready=(0, 4, 8, 12) if first and i == 0 else ())
                slab(actB, ready={c: 2 for c in range(8)})

            def mlp():
                norm_transposes()
                before = dict(C.n)
                mlp_slab(True)
                before[act_split] += 8
                with C.loop(2, before, 1):
                    mlp_slab(False)
                mlp_slab(False)

            mlp()

            norm_transposes()
            column_block(0, actA, ready={0: 4, 4: 4})

            def k_transposes():
                e.wait_ge(k_turned, C.next(k_turned))
                for h in range(NH):
                    transposes(6 + h, [qtok[:, h, i * P:(i + 1) * P] for i in range(4)])

            def q_transposes():
                e.wait_ge(q_turned, C.next(q_turned))
                if C.any(o_split):
                    e.wait_ge(o_split, C.now(o_split))
                for h in range(NH):
                    transposes(6 + h, [qtok[:, h, i * P:(i + 1) * P] for i in range(4)])

            def scores(b, c, j):
                kv = 2 * b + j
                if c == 0:
                    fill(4)
                    e.matmul(ps[:, 4, :].rearrange("p (h n) -> p h n", h=4), ident_r[:, :],
                             amask_r[:, 1, :].unsqueeze(1).broadcast_to([P, 4, P]), start=True, stop=False)
                    for i in range(4):
                        last = e.matmul(ps[:, 4, i * P:(i + 1) * P], qT[:, i, 0:P], kz[:, kv, 0:P],
                                        start=False, stop=(i == 3))
                    last.then_inc(full[4], C.up(full[4]))
                    return
                for half in range(2):
                    fill(4 + half)
                    e.matmul(ps[:, 4 + half, :].rearrange("p (h n) -> p h n", h=2), ident_r[:, :],
                             amask_r[:, :, :].rearrange("p a n -> p (a n)").unsqueeze(1).broadcast_to([P, 2, 2 * P]),
                             start=True, stop=False)
                    for i in range(2):
                        last = e.matmul(ps[:, 4 + half, i * T:(i + 1) * T], qT[:, 2 * half + i, P:T], kz[:, kv, :],
                                        start=False, stop=(i == 1))
                    last.then_inc(full[4 + half], C.up(full[4 + half]))

            def p_transposes(c):
                e.wait_ge(exps_ready, C.next(exps_ready))
                if c == 0:
                    transposes(6, [pb[:, i, 0:P] for i in range(4)])
                else:
                    e.wait_ge(o_split, C.now(o_split))
                    for half in range(2):
                        transposes(6 + half, [pb[:, 2 * half + i // 2, (i % 2) * P:(i % 2 + 1) * P] for i in range(4)])

            def values(b, c, j):
                kv = 2 * b + j
                if c:
                    emptied(7)
                fill(6)
                for i in range(4):
                    for kc in range(1 + c):
                        last = e.matmul(ps[:, 6, i * HD:(i + 1) * HD], pT[:, (1 + c) * i + kc, :],
                                        vtok[:, kc, kv * HD:(kv + 1) * HD], start=(kc == 0), stop=(kc == c))
                last.then_inc(full[6], C.up(full[6]))

            def o_transposes():
                emptied(6)
                C.n[o_split] += 1
                transposes(7, [otok[:, i * P:(i + 1) * P] for i in range(4)], counted=False)

            UNITS = [(0, 0), (0, 1), (1, 0), (1, 1)]

            def attention(b, between):
                between = list(between)

                def go(k):
                    for f in between[:k]:
                        f()
                    del between[:k]

                go(3)
                q_transposes()
                go(1)
                emptied(6)
                emptied(7)
                scores(b, *UNITS[0])
                go(2)
                for u, (c, j) in enumerate(UNITS):
                    p_transposes(c)
                    if u < 3:
                        scores(b, *UNITS[u + 1])
                    if u % 2 == 0:
                        go(1)
                    values(b, c, j)
                    if j == 1:
                        o_transposes()
                go(8)

            column_block(2, actA, after={3: [k_transposes]})
            column_block(0, actA)
            for b in range(QB):
                b0 = 2 * ((b + 1) % 2)
                if b < QB - 1:
                    fill(b0)
                    fill(b0 + 1)
                    attention(b, [lambda c=c: column_chunk_products(b0, actA, c) for c in range(8)])
                else:
                    e.wait_ge(o_split, C.now(o_split))
                    fill(0)
                    fill(1)
                    attention(b, [lambda c=c: column_chunk_products(0, actB, c) for c in range(6)])
                    e.wait_ge(o_split, C.now(o_split))
                    for c in (6, 7):
                        column_chunk_products(0, actB, c)
            for nb in range(1, 4):
                column_block(2 * (nb % 2), actB)
            mlp()


        @block.scalar
        def _(e):
            C = Counts(e, by_dma)
            C.n[w_used] = -1

            def split_weights():
                i = C.n[w_hi_done]
                if i < TOTAL:
                    s, r = i % RING, i % RAW
                    e.wait_ge(loaded[r], C.next(loaded[r]))
                    e.activation(whi[:, s, :], raw[:, r, :], ACT.Copy).then_inc(w_hi_done, C.up(w_hi_done))

            def step():
                C.n[w_used] += 1
                if C.n[w_hi_done] < TOTAL and C.any(w_used, back=RING - 1 - LEAD):
                    e.wait_ge(w_used, C.now(w_used, back=RING - 1 - LEAD))
                split_weights()

            def products():
                e.wait_ge(w_used, C.now(w_used))

            def hi(dst, src):
                e.activation(dst, src, ACT.Copy).then_inc(act_hi_done, C.up(act_hi_done))

            def tiles(b):
                return ps[:, b, :].rearrange("p (t n) -> p t n", n=P)

            for h in range(NH):
                e.dma_start(xin[:, h, :], t["x"][0, h * P:(h + 1) * P, :]).then_inc(x_in, C.up(x_in))
            for dst, src in ((vst[0:48, 0:4, :], t["conv_w"][0].rearrange("k (t p) -> t k p", p=P)),
                             (vst[0:48, 4, :], t["conv_b"][0].rearrange("(t p) -> t p", p=P)),
                             (nst[0:32, :], t["norm_w"][0].rearrange("(t p) -> t p", p=P)),
                             (gst[0:64, 0, :], t["ln_g"].rearrange("a b (t p) -> (a b t) p", p=P)),
                             (gst[0:64, 1, :], t["ln_b"].rearrange("a b (t p) -> (a b t) p", p=P)),
                             (sink[:, :], t["sinks"].broadcast_to([P, 32]))):
                e.dma_start(dst, src).then_inc(vectors_in, C.up(vectors_in))
            for dst, src in ((dtb, t["dt_bias"]), (alg, t["A_log"]), (Dsk, t["Dskip"])):
                e.dma_start(dst[:, :], src.broadcast_to([P, NHD])).then_inc(per_head_in, C.up(per_head_in))

            e.wait_ge(consts_in, C.next(consts_in))
            e.activation(ident_r[:, :], kst[:, K_ID:K_ID + P], ACT.Copy)
            e.activation(smask_r[:, :], kst[:, K_SMASK:K_SMASK + P], ACT.Copy)
            e.activation(amask_r[:, :, :].rearrange("p a n -> p (a n)"), kst[:, K_AMASK:K_AMASK + 2 * P], ACT.Copy)
            e.activation(sel2[:, :], kst[:, K_SEL:K_SEL + NHD], ACT.Copy).then_inc(selection_ready, C.up(selection_ready))
            e.wait_ge(per_head_in, C.now(per_head_in))
            e.activation(eA[:, :], alg[:, :], ACT.Exp)

            C.n[full[0]] += 1
            C.n[full[1]] += 1
            for g in range(4):
                for h in range(NH):
                    b = (2 + 2 * g + h) % 8
                    e.wait_ge(full[b], C.next(full[b]))
                    hi(actA[:, 4 * g:4 * g + 4, 0, h * P:(h + 1) * P], tiles(b))
                if g == 0:
                    for _ in range(LEAD):
                        split_weights()

            step()
            e.wait_ge(nab_ready, C.next(nab_ready))
            e.activation(dv[:, 2, :], dv[:, 1, :], ACT.Exp).then_inc(uexp_ready, C.up(uexp_ready))

            def dt_decays():
                e.wait_ge(cs_ready, C.next(cs_ready))
                e.activation(ecs[:, :], dv[:, 9, NHD:2 * NHD], ACT.Exp)
                e.wait_ge(full[5], C.next(full[5]))
                e.activation(te[:, :], ps[:, 5, 0:NHD], ACT.Exp).then_inc(free[5], C.up(free[5]))

            def dt_cs2():
                e.wait_ge(full[6], C.next(full[6]))
                e.activation(cs2[:, :, :].rearrange("p c n -> p (c n)"), ps[:, 6, 0:T], ACT.Copy)
                e.activation(ncs2[:, :, :].rearrange("p c n -> p (c n)"), ps[:, 6, 0:T], ACT.Copy,
                                           scale=-1.0).then_inc(free[6], C.up(free[6]))

            def cross(i, b0=0, buf=crossb):
                products()
                e.activation(buf[:, i % 2, :], ps[:, b0 + i % 2, T:2 * T], ACT.Copy).then_inc(cross_out, C.up(cross_out))

            def tanh(i):
                e.wait_ge(conv_done, C.next(conv_done))
                e.activation(thb[:, i % 2, :], xh[:, i % 2, :], ACT.Tanh).then_inc(tanh_done, C.up(tanh_done))

            def z_tanh():
                products()
                for c in range(NH):
                    e.activation(yb[:, c, :], ps[:, 2 + c, :], ACT.Tanh, scale=0.5).then_inc(
                        z_tanh_done, C.up(z_tanh_done))

            def a1():
                e.wait_ge(full[6], C.next(full[6]))
                e.activation(bcb[:, :, :].rearrange("p a n -> p (a n)"), ps[:, 6, 0:3 * P], ACT.Copy).then_inc(
                    free[6], C.up(free[6]))

            def decay(c):
                for hh, b in ((0, 7), (1, 6)):
                    e.wait_ge(full[b], C.next(full[b]))
                    e.activation(em[:, c, hh * BLK:(hh + 1) * BLK], ps[:, b, :], ACT.Exp).then_inc(free[b], C.up(free[b]))

            def a4():
                e.wait_ge(full[4], C.next(full[4], 2))
                e.activation(st[:, :], ps[:, 4, :], ACT.Copy).then_inc(free[4], C.up(free[4]))
                C.n[full[4]] += 1

            def square(c):
                e.wait_ge(y_ready, C.next(y_ready))
                e.activation(em[:, c, 0:GW], yb[:, c, :], ACT.Square, accum_out=ss[:, c:c + 1]).then_inc(
                    y_squared, C.up(y_squared))
                if c:
                    C.n[full[6]] += 1
                    C.n[full[7]] += 1

            def scale_y():
                e.wait_ge(rstd_ready, C.next(rstd_ready))
                for c in range(NH):
                    e.activation(xdt[:, c, :], yb[:, c, :], ACT.Copy, scale=rstd[:, c:c + 1]).then_inc(
                        y_normed, C.up(y_normed))

            def group(carry, ssd, first=False):
                step()
                if carry:
                    z_tanh()
                step()
                step()
                cross(0)
                if first:
                    dt_decays()
                step()
                tanh(0)
                if ssd:
                    a1()
                step()
                cross(1)
                if ssd:
                    decay(0)
                step()
                tanh(1)
                step()
                cross(2)
                if ssd:
                    decay(1)
                step()
                tanh(2)
                if first:
                    dt_cs2()
                step()
                cross(3)
                if ssd:
                    a4()
                step()
                tanh(3)
                step()
                cross(4)
                step()
                tanh(4)
                if ssd:
                    square(0)
                step()
                cross(5)
                step()
                tanh(5)
                if ssd:
                    square(1)
                step()
                if ssd:
                    scale_y()
                for _ in range(5):
                    step()

            C.n[full[4]] += 1
            group(False, False, first=True)
            before = dict(C.n)
            group(True, True)
            with C.loop(3, before, 2):
                group(True, True)
                group(True, True)

            def split_y(lo_half):
                act = act1 if lo_half else actA
                for g in range(4):
                    hi(act[:, 4 * g:4 * g + 4, 0, :], yT[:, 16 * lo_half + 4 * g:16 * lo_half + 4 * g + 4, :])

            step()
            z_tanh()
            split_y(0)
            a1()
            step()
            decay(0)
            step()
            decay(1)
            step()
            step()
            a4()
            step()
            square(0)
            step()
            square(1)
            scale_y()
            step()
            step()
            e.wait_ge(yT_done, C.next(yT_done))
            split_y(1)
            for _ in range(2 * SLAB_CHUNKS - 9):
                step()

            C.n[act_split] += 2 * 8

            def norm(l):
                e.wait_ge(rstd_ready, C.next(rstd_ready))
                for g in range(4):
                    r = res[:, 1, g * BLK:(g + 1) * BLK]
                    e.activation(r, r, ACT.Identity, bias=nmr[:, 1:2], scale=rstd[:, 1:2]).then_inc(
                        h1_normed, C.up(h1_normed))
                for g in range(4):
                    e.wait_ge(full[g], C.next(full[g]))
                    if g:
                        e.wait_ge(act_split, C.next(act_split, 2))
                    for i in range(4):
                        kt = 4 * g + i
                        last = e.activation(hf[:, 1, i * P:(i + 1) * P], ps[:, g, i * P:(i + 1) * P], ACT.Identity,
                                            bias=lnb[:, l, kt:kt + 1], scale=lng[:, l, kt:kt + 1])
                    last.then_inc(h1_affine, C.up(h1_affine))
                    e.wait_ge(h0_affine, C.next(h0_affine))
                    for h in range(NH):
                        if h == 1:
                            e.wait_ge(h1_affine, C.now(h1_affine))
                        hi(actA[:, 4 * g:4 * g + 4, 0, h * P:(h + 1) * P],
                           hf[:, h, :].rearrange("p (t n) -> p t n", n=P))
                C.n[act_split] += 2

            def f_hi(i):
                e.wait_ge(f_squared, C.next(f_squared))
                hi(actB[:, i, 0, :], fsq[:, i % 2, :])

            def mlp_slab():
                for i in range(SLAB_CHUNKS):
                    step()
                    if i and i % 2 == 0:
                        cross(i // 2 - 1, 4, mcross)
                    if i > 1 and i % 2:
                        f_hi(i // 2 - 1)
                for i in range(SLAB_CHUNKS):
                    step()
                    if i == 0:
                        cross(15, 4, mcross)
                    if i == 1:
                        f_hi(15)

            def mlp(l):
                norm(l)
                before = dict(C.n)
                mlp_slab()
                with C.loop(2, before, 1):
                    mlp_slab()
                mlp_slab()

            mlp(0)

            C.n[act_split] += 4 * 16
            norm(1)
            for b, k in FULLS.items():
                C.n[full[b]] = k

            def kz_out():
                for h in range(NH):
                    e.wait_ge(full[6 + h], C.next(full[6 + h]))
                    for j in range(2):
                        rows = slice(j * HD, (j + 1) * HD)
                        last = e.activation(kz[rows, :, h * P:(h + 1) * P].rearrange("p (t j) n -> p t j n", j=2)[:, :, j, :],
                                            tiles(6 + h)[rows, :, :], ACT.Copy)
                    last.then_inc(free[6 + h], C.up(free[6 + h]))

            def qT_out():
                for h in range(NH):
                    e.wait_ge(full[6 + h], C.next(full[6 + h]))
                    e.activation(qT[:, :, h * P:(h + 1) * P], tiles(6 + h), ACT.Copy).then_inc(
                        free[6 + h], C.up(free[6 + h]))

            def exps(c):
                e.wait_ge(maxima_ready, C.next(maxima_ready))
                for i in range(4):
                    b = 4 + (i // 2 if c else 0)
                    if c and i % 2 == 0 or i == 0:
                        e.wait_ge(full[b], C.next(full[b]))
                    w = T if c else P
                    k = (i % 2) * T if c else i * P
                    ins = e.activation(pb[:, i, 0:w], ps[:, b, k:k + w], ACT.Exp, bias=nm[:, i:i + 1], scale=SCALE,
                                       accum_out=rs[:, i:i + 1])
                    if c and i % 2 or i == 3:
                        ins.then_inc(free[b], C.up(free[b]))
                e.activation(es[:, :], sb_[:, :], ACT.Exp).then_inc(exps_ready, C.up(exps_ready))

            def pT_out():
                e.wait_ge(full[6], C.next(full[6]))
                e.activation(pT[:, 0:4, :], tiles(6), ACT.Copy).then_inc(free[6], C.up(free[6]))

            def attention(b, k=8):
                steps = iter(range(k))

                def go(n=1):
                    for _ in range(n):
                        if next(steps, None) is not None:
                            step()

                go(4)
                qT_out()
                go(2)
                for c, j in ((0, 0), (0, 1), (1, 0), (1, 1)):
                    exps(c)
                    pT_out()
                    if c:
                        C.n[full[7]] += 1
                    if j == 0:
                        go()
                    C.n[full[6]] += 1
                    if j:
                        e.wait_ge(full[7], C.next(full[7]))
                        hi(actB[:, 4 * b:4 * b + 4, 0, c * P:(c + 1) * P], tiles(7))
                go(8)

            for i in range(8):
                step()
            for i in range(8):
                step()
                if i == 3:
                    kz_out()
            for i in range(8):
                step()
            e.wait_ge(res_ready, C.next(res_ready, 3))
            for b in range(QB):
                attention(b)
            for i in range(SLAB_CHUNKS - 8):
                step()
            mlp(2)

        @block.vector
        def _(e):
            C = Counts(e, by_dma)
            C.n[w_used] = -1

            def split_weights():
                i = C.n[w_split]
                if i < TOTAL:
                    s, r = i % RING, i % RAW
                    e.wait_ge(w_hi_done, C.next(w_hi_done))
                    e.tensor_tensor(wlo[:, s, :], raw[:, r, :], whi[:, s, :].bitcast(F32), ALU.subtract).then_inc(
                        w_split, C.up(w_split))

            def step():
                C.n[w_used] += 1
                split_weights()

            def products():
                e.wait_ge(w_used, C.now(w_used))

            def lo(dst, src, hi_part, done=act_split):
                e.wait_ge(act_hi_done, C.next(act_hi_done))
                e.tensor_tensor(dst, src, hi_part.bitcast(F32), ALU.subtract).then_inc(done, C.up(done))

            def tiles(b):
                return ps[:, b, :].rearrange("p (t n) -> p t n", n=P)

            def heads(x, n=GH):
                return x.rearrange("p (h d) -> p h d", h=n)

            def per_head(x, g):
                return x[:, bass.ds(g * GH, GH)].unsqueeze(2).broadcast_to([P, GH, HD])

            e.wait_ge(consts_in, C.next(consts_in))
            e.tensor_copy(ident[:, :], kst[:, K_ID:K_ID + P]).then_inc(dve_step, C.up(dve_step))
            e.wait_ge(dve_step, C.now(dve_step))
            e.tensor_copy(cosb[:, :, :].rearrange("p c n -> p (c n)"), kst[:, K_COS:K_COS + 64])
            e.tensor_copy(sinb[:, :, :].rearrange("p c n -> p (c n)"), kst[:, K_SIN:K_SIN + 64])
            e.memset(xpad[:, :, 0:3], 0.0)
            e.wait_ge(full[0], C.next(full[0]))
            cwv = cw[:, :].rearrange("p (g s k) -> p g s k", g=NG, s=6)
            for k in range(5):
                src = ps[:, 0, k * 48:(k + 1) * 48]
                e.tensor_scalar(cwv[:, :, 2:6, k], src[:, 0:32].rearrange("p (g s) -> p g s", s=4), 0.5, None, ALU.mult)
                e.tensor_scalar(cwv[:, :, 0, k], src[:, 32:40], 0.5, None, ALU.mult)
                e.tensor_scalar(cwv[:, :, 1, k], src[:, 40:48], 0.5, None, ALU.mult)
            e.tensor_copy(nw[:, :], ps[:, 0, 240:272]).then_inc(free[0], C.up(free[0]))
            e.wait_ge(full[1], C.next(full[1]))
            e.tensor_copy(lng[:, :, :].rearrange("p a t -> p (a t)"), ps[:, 1, 0:64])
            e.tensor_copy(lnb[:, :, :].rearrange("p a t -> p (a t)"), ps[:, 1, 64:128]).then_inc(free[1], C.up(free[1]))

            for g in range(4):
                for h in range(NH):
                    b = (2 + 2 * g + h) % 8
                    e.wait_ge(full[b], C.next(full[b]))
                    tk = slice(h * P, (h + 1) * P)
                    lo(actA[:, 4 * g:4 * g + 4, 1, tk], tiles(b), actA[:, 4 * g:4 * g + 4, 0, tk])
                if g == 0:
                    for _ in range(LEAD):
                        split_weights()

            step()
            C.n[w_used] += 1
            products()
            C.n[w_used] -= 1
            e.wait_ge(per_head_in, C.next(per_head_in, 3))
            v, nab, u, den_, rec, s_, s2_, q_, lp, cs, dA = [dv[:, i, :] for i in (0, 1, 2, 3, 4, 5, 6, 7, 8, 9, 11)]
            for h in range(NH):
                e.tensor_tensor(dv[:, 0, h * NHD:(h + 1) * NHD], ps[:, 2 + h, 0:NHD], dtb[:, :],
                                                     ALU.add).then_inc(free[2 + h], C.up(free[2 + h]))
            e.wait_ge(free[3], C.now(free[3]))
            e.scalar_tensor_tensor(nab, v, -1.0, v, ALU.mult, ALU.min).then_inc(nab_ready, C.up(nab_ready))
            e.wait_ge(uexp_ready, C.next(uexp_ready))
            e.tensor_scalar(den_, u, 2.0, None, ALU.add).then_inc(dve_step, C.up(dve_step))
            e.wait_ge(dve_step, C.now(dve_step))
            e.reciprocal(rec, den_).then_inc(dve_step, C.up(dve_step))
            e.wait_ge(dve_step, C.now(dve_step))
            e.tensor_tensor(s_, u, rec, ALU.mult).then_inc(dve_step, C.up(dve_step))
            e.wait_ge(dve_step, C.now(dve_step))
            e.tensor_tensor(s2_, s_, s_, ALU.mult).then_inc(dve_step, C.up(dve_step))
            e.wait_ge(dve_step, C.now(dve_step))
            e.tensor_scalar(q_, s2_, 1.0 / 15, None, ALU.mult).then_inc(dve_step, C.up(dve_step))
            e.wait_ge(dve_step, C.now(dve_step))
            for k in (13, 11, 9, 7, 5, 3):
                e.scalar_tensor_tensor(q_, q_, 1.0 / k, s2_, ALU.add, ALU.mult).then_inc(dve_step, C.up(dve_step))
                e.wait_ge(dve_step, C.now(dve_step))
            e.scalar_tensor_tensor(lp, q_, 1.0, s_, ALU.add, ALU.mult).then_inc(dve_step, C.up(dve_step))
            e.wait_ge(dve_step, C.now(dve_step))
            e.tensor_scalar(lp, lp, 2.0, None, ALU.mult).then_inc(dve_step, C.up(dve_step))
            e.wait_ge(dve_step, C.now(dve_step))
            dtf = dt[:, :, :].rearrange("p c h -> p (c h)")
            e.scalar_tensor_tensor(dtf, v, 0.0, lp, ALU.max, ALU.add).then_inc(dve_step, C.up(dve_step))
            e.wait_ge(dve_step, C.now(dve_step))
            e.scalar_tensor_tensor(
                dv[:, 11, :].rearrange("p (c h) -> p c h", c=NH), dt[:, :, :], -1.0,
                eA[:, :].unsqueeze(1).broadcast_to([P, NH, NHD]), ALU.mult, ALU.mult).then_inc(dt_ready, C.up(dt_ready))

            def dt_sums():
                e.wait_ge(full[4], C.next(full[4]))
                e.tensor_copy(cs, ps[:, 4, 0:2 * NHD]).then_inc(free[4], C.up(free[4]))
                e.wait_ge(free[4], C.now(free[4]))
                e.tensor_copy(csr[:, :, :], cs.rearrange("p (c h) -> p c h", c=NH)).then_inc(cs_ready, C.up(cs_ready))
                e.wait_ge(cs_ready, C.now(cs_ready))
                e.tensor_copy(cshl[:, :, 0, :], csr[:, :, :].bitcast(F32))
                e.tensor_tensor(cshl[:, :, 1, :], cs.rearrange("p (c h) -> p c h", c=NH),
                                             csr[:, :, :].bitcast(F32), ALU.subtract).then_inc(cs_split, C.up(cs_split))
                C.n[free[5]] += 1
                C.n[full[5]] += 1
                C.n[free[6]] += 1
                C.n[full[6]] += 1

            def conv(i, par):
                x = i % 2
                w = [cwg[:, par, i * 5 + k:i * 5 + k + 1] for k in range(5)]
                e.wait_ge(cross_out, C.next(cross_out))
                e.tensor_tensor(xpad[:, x, 3:3 + T], ps[:, x, 0:T], crossb[:, x, :], ALU.add).then_inc(
                    free[x], C.up(free[x]))
                e.wait_ge(free[x], C.now(free[x]))
                e.tensor_scalar(xh[:, x, :], xpad[:, x, 3:3 + T], w[3], w[4], ALU.mult, ALU.add).then_inc(
                    dve_step, C.up(dve_step))
                e.wait_ge(dve_step, C.now(dve_step))
                for k in (2, 1):
                    e.scalar_tensor_tensor(xh[:, x, :], xpad[:, x, k:k + T], w[k], xh[:, x, :], ALU.mult, ALU.add).then_inc(
                        dve_step, C.up(dve_step))
                    e.wait_ge(dve_step, C.now(dve_step))
                e.scalar_tensor_tensor(xh[:, x, :], xpad[:, x, 0:T], w[0], xh[:, x, :], ALU.mult, ALU.add).then_inc(
                    conv_done, C.up(conv_done))

            def silu(i, par):
                e.wait_ge(tanh_done, C.next(tanh_done))
                e.scalar_tensor_tensor(xT[:, par, i, :], thb[:, i % 2, :], 1.0, xh[:, i % 2, :],
                                                  ALU.add, ALU.mult).then_inc(xT_ready, C.up(xT_ready))

            def z_out():
                for c in range(NH):
                    e.wait_ge(z_tanh_done, C.next(z_tanh_done))
                    e.scalar_tensor_tensor(zs[:, c, :], yb[:, c, :], 1.0, ps[:, 2 + c, :],
                                                                ALU.add, ALU.mult).then_inc(
                                                                    free[2 + c], C.up(free[2 + c]))

            def d1(c, g):
                e.wait_ge(full[4 + c], C.next(full[4 + c]))
                e.tensor_tensor(heads(xdt[:, c, :]), heads(ps[:, 4 + c, :]), per_head(dt[:, c, :], g),
                                                 ALU.mult).then_inc(dve_step, C.up(dve_step))
                e.tensor_tensor(heads(xD[:, c, :]), heads(ps[:, 4 + c, :]), per_head(Dsk, g),
                                                     ALU.mult).then_inc(free[4 + c], C.up(free[4 + c]))
                if c:
                    e.wait_ge(dve_step, C.now(dve_step))
                    e.tensor_tensor(heads(xde[:, :]), heads(xdt[:, 0, :]), per_head(te, g), ALU.mult).then_inc(
                        xdt_ready, C.up(xdt_ready))

            def d23(c):
                e.wait_ge(free[7], C.next(free[7]))
                e.wait_ge(free[6], C.next(free[6], 1 if c else 2))
                C.n[full[7]] += 1
                C.n[full[6]] += 1 if c else 2
                x = em[:, c, :].rearrange("p (h n) -> p h n", h=GH)
                e.tensor_tensor(x, x, bcb[:, 1 + c, :].unsqueeze(1).broadcast_to([P, GH, P]), ALU.mult).then_inc(
                    m_ready, C.up(m_ready))

            def gate(c):
                e.scalar_tensor_tensor(yb[:, c, :], yb[:, c, :], 0.5, zs[:, c, :], ALU.mult, ALU.mult).then_inc(
                    y_ready, C.up(y_ready))

            def d4():
                e.wait_ge(full[5], C.next(full[5]))
                e.tensor_tensor(yb[:, 0, :], ps[:, 5, :], xD[:, 0, :], ALU.add).then_inc(free[5], C.up(free[5]))
                e.wait_ge(free[5], C.now(free[5]))
                gate(0)
                C.n[free[4]] += 1
                C.n[full[4]] += 1

            def d5(g):
                e.wait_ge(full[6], C.next(full[6]))
                e.tensor_tensor(heads(xde[:, :]), heads(ps[:, 6, :]), per_head(ecs, g), ALU.mult).then_inc(
                    free[6], C.up(free[6]))
                e.wait_ge(free[6], C.now(free[6]))
                e.tensor_tensor(xde[:, :], xde[:, :], xD[:, 1, :], ALU.add).then_inc(dve_step, C.up(dve_step))
                e.wait_ge(dve_step, C.now(dve_step))
                e.wait_ge(full[7], C.next(full[7]))
                e.tensor_tensor(yb[:, 1, :], ps[:, 7, :], xde[:, :], ALU.add).then_inc(free[7], C.up(free[7]))
                e.wait_ge(free[7], C.now(free[7]))
                gate(1)

            def d8(c, g):
                e.wait_ge(full[4 + c], C.next(full[4 + c]))
                e.tensor_tensor(
                    yT[:, bass.ds(4 * g, 4), c * P:(c + 1) * P], tiles(4 + c),
                    nw[:, bass.ds(4 * g, 4)].unsqueeze(2).broadcast_to([P, 4, P]), ALU.mult).then_inc(
                        free[4 + c], C.up(free[4 + c]))

            def group(g, par, carry, ssd, first=False):
                step()
                e.tensor_copy(cwg[:, par, :], cw[:, bass.ds(g * 30, 30)]).then_inc(dve_step, C.up(dve_step))
                e.wait_ge(dve_step, C.now(dve_step))
                if carry:
                    silu(5, 1 - par)
                step()
                if first:
                    dt_sums()
                if carry:
                    z_out()
                step()
                conv(0, par)
                step()
                if ssd:
                    d1(0, g - 1)
                step()
                silu(0, par)
                if ssd:
                    d1(1, g - 1)
                step()
                conv(1, par)
                step()
                if ssd:
                    d23(0)
                step()
                silu(1, par)
                conv(2, par)
                step()
                if ssd:
                    d23(1)
                step()
                silu(2, par)
                conv(3, par)
                step()
                if ssd:
                    d4()
                step()
                silu(3, par)
                conv(4, par)
                step()
                if ssd:
                    d5(g - 1)
                step()
                silu(4, par)
                conv(5, par)
                for _ in range(5):
                    step()
                if ssd:
                    d8(0, g - 1)
                step()
                if ssd:
                    d8(1, g - 1)

            group(0, 0, False, False, first=True)
            before = dict(C.n)
            group(1, 1, True, True)
            with C.loop(3, before, 2) as i:
                group(2 * i + 2, 0, True, True)
                group(2 * i + 3, 1, True, True)

            def split_y(half):
                act = act1 if half else actA
                for g in range(4):
                    lo(act[:, 4 * g:4 * g + 4, 1, :], yT[:, 16 * half + 4 * g:16 * half + 4 * g + 4, :],
                       act[:, 4 * g:4 * g + 4, 0, :])

            def add_block(nb, stats=False):
                products()
                for h in range(NH):
                    b = 2 * (nb % 2) + h
                    r = res[:, h, nb * BLK:(nb + 1) * BLK]
                    e.tensor_tensor(r, ps[:, b, :], r, ALU.add).then_inc(free[b], C.up(free[b]))
                if stats:
                    for h in range(NH):
                        e.wait_ge(free[2 * (nb % 2) + h], C.now(free[2 * (nb % 2) + h]))
                        e.bn_stats(bst[:, h, nb * 6:(nb + 1) * 6], res[:, h, nb * BLK:(nb + 1) * BLK]).then_inc(
                            dve_step, C.up(dve_step))

            def after_products(f):
                C.n[w_used] += 1
                f()
                C.n[w_used] -= 1

            g7 = NG - 1
            step()
            silu(5, 1)
            split_y(0)
            z_out()
            d1(0, g7)
            d1(1, g7)
            step()
            d23(0)
            step()
            d23(1)
            step()
            step()
            d4()
            step()
            d5(g7)
            step()
            step()
            d8(0, g7)
            d8(1, g7)
            e.memset(small[:, 95:96], 0.0).then_inc(yT_done, C.up(yT_done))
            step()
            split_y(1)
            e.wait_ge(res_ready, C.next(res_ready))
            for i in range(8, 2 * SLAB_CHUNKS):
                if i > 8:
                    step()
                if i % 8 == 0:
                    add_block(i // 8 % 4 + (-1 if i // 8 % 4 else 3), stats=i > SLAB_CHUNKS)
            after_products(lambda: add_block(3, stats=True))

            def mean_and_variance():
                for h in range(NH):
                    e.wait_ge(dve_step, C.now(dve_step))
                    e.bn_aggr(mvb[:, h, :], bst[:, h, :]).then_inc(mean_var_ready, C.up(mean_var_ready))
                e.wait_ge(mean_var_ready, C.now(mean_var_ready))

            def norm(l):
                mean_and_variance()
                e.wait_ge(rstd_ready, C.next(rstd_ready))
                for g in range(4):
                    r = res[:, 0, g * BLK:(g + 1) * BLK]
                    e.tensor_scalar(r, r, mvb[:, 0, 0:1], rstd[:, 0:1], ALU.subtract, ALU.mult).then_inc(
                        h0_normed, C.up(h0_normed))
                for g in range(4):
                    e.wait_ge(full[4 + g], C.next(full[4 + g]))
                    if g:
                        e.wait_ge(act_split, C.now(act_split))
                    for i in range(4):
                        kt = 4 * g + i
                        last = e.tensor_scalar(hf[:, 0, i * P:(i + 1) * P], ps[:, 4 + g, i * P:(i + 1) * P],
                                               lng[:, l, kt:kt + 1], lnb[:, l, kt:kt + 1], ALU.mult, ALU.add)
                    last.then_inc(h0_affine, C.up(h0_affine))
                    for h in range(NH):
                        tk = slice(h * P, (h + 1) * P)
                        lo(actA[:, 4 * g:4 * g + 4, 1, tk], hf[:, h, :].rearrange("p (t n) -> p t n", n=P),
                           actA[:, 4 * g:4 * g + 4, 0, tk])

            def last_norm():
                mean_and_variance()
                e.wait_ge(gains_in, C.next(gains_in, 8))
                for h in range(NH):
                    pieces = [cols for hh, cols in OUTPUT_PIECES if hh == h]
                    for cols in pieces:
                        e.scalar_tensor_tensor(res[:, h, cols], res[:, h, cols], mvb[:, h, 0:1], gb[:, 0, cols],
                                               ALU.subtract, ALU.mult).then_inc(centred, C.up(centred))
                    if h == 0:
                        e.wait_ge(rstd_ready, C.next(rstd_ready))
                    e.wait_ge(centred, C.now(centred))
                    for cols in pieces:
                        e.scalar_tensor_tensor(res[:, h, cols], res[:, h, cols], rstd[:, h:h + 1], gb[:, 1, cols],
                                               ALU.mult, ALU.add).then_inc(output_ready, C.up(output_ready))

            def relu2(i):
                b = 4 + i % 2
                e.wait_ge(cross_out, C.next(cross_out))
                e.tensor_tensor(fb[:, i % 2, :], ps[:, b, 0:T], mcross[:, i % 2, :], ALU.add).then_inc(
                    free[b], C.up(free[b]))
                e.wait_ge(free[b], C.now(free[b]))
                e.scalar_tensor_tensor(fsq[:, i % 2, :], fb[:, i % 2, :], 0.0, fb[:, i % 2, :],
                                                   ALU.max, ALU.mult).then_inc(f_squared, C.up(f_squared))

            def f_lo(i):
                lo(actB[:, i, 1, :], fsq[:, i % 2, :], actB[:, i, 0, :])

            def mlp_slab(stats=False, first=False):
                for i in range(SLAB_CHUNKS):
                    step()
                    if i and i % 2 == 0:
                        relu2(i // 2 - 1)
                    if i > 1 and i % 2:
                        f_lo(i // 2 - 1)
                for i in range(SLAB_CHUNKS):
                    step()
                    if i == 0:
                        relu2(15)
                    if i == 1:
                        f_lo(15)
                    if i == 8 and first:
                        e.wait_ge(res_ready, C.next(res_ready))
                    if i and i % 8 == 0:
                        add_block(i // 8 - 1, stats)
                after_products(lambda: add_block(3, stats))

            def mlp():
                before = dict(C.n)
                mlp_slab(first=True)
                before[res_ready] = before.get(res_ready, 0) + 1
                with C.loop(2, before, 1):
                    mlp_slab()
                mlp_slab(stats=True)

            C.n[rstd_ready] += NG
            norm(0)
            mlp()
            norm(1)
            assert all(C.n[full[b]] == k for b, k in FULLS.items())

            def rope(b0):
                products()
                for h in range(NH):
                    x = ps[:, b0 + h, :].rearrange("p (h a d) -> p h a d", a=2, d=32)
                    c_ = cosb[:, h, :].unsqueeze(1).unsqueeze(1).broadcast_to([P, 8, 2, 32])
                    s = sinb[:, h, :].unsqueeze(1).broadcast_to([P, 8, 32])
                    xa = ropeA[:, :].rearrange("p (h a d) -> p h a d", a=2, d=32)
                    xb = ropeB[:, :].rearrange("p (h a d) -> p h a d", a=2, d=32)
                    e.wait_ge(dve_step, C.now(dve_step))
                    e.tensor_tensor(xa, x, c_, ALU.mult)
                    e.tensor_tensor(xb[:, :, 0, :], x[:, :, 1, :], s, ALU.mult)
                    e.tensor_tensor(xb[:, :, 1, :], x[:, :, 0, :], s, ALU.mult).then_inc(free[b0 + h], C.up(free[b0 + h]))
                    e.wait_ge(free[b0 + h], C.now(free[b0 + h]))
                    for a, op in ((0, ALU.subtract), (1, ALU.add)):
                        yield h, a, xa, xb, op

            def k_rope():
                for h, a, xa, xb, op in rope(0):
                    ins = e.tensor_tensor(qtok[:, h, :].rearrange("p (h a d) -> p h a d", a=2, d=32)[:, :, a, :],
                                          xa[:, :, a, :], xb[:, :, a, :], op)
                    if a == 0:
                        ins.then_inc(dve_step, C.up(dve_step))
                    elif h == 0:
                        ins.then_inc(dve_step, C.up(dve_step))
                ins.then_inc(k_turned, C.up(k_turned))

            def q_rope(b0):
                for h, a, xa, xb, op in rope(b0):
                    for j in range(2):
                        o = qtok[:, h, :].rearrange("p (t j a d) -> p t j a d", j=2, a=2, d=32)[:, :, j, a, :]
                        ins = e.tensor_tensor(o, xa[:, 4 * j:4 * j + 4, a, :], xb[:, 4 * j:4 * j + 4, a, :], op)
                        if not (h == 1 and a == 1 and j == 1):
                            ins.then_inc(dve_step, C.up(dve_step))
                ins.then_inc(q_turned, C.up(q_turned))

            def maxima(b, c, j):
                for k in range(1 + c):
                    e.wait_ge(full[4 + k], C.next(full[4 + k]))
                w = T if c else P
                src = ps[:, 4:5 + c, :].rearrange("p a (h n) -> p (a h) n", n=w)
                e.tensor_reduce(mx, src, AX.X, ALU.max).then_inc(dve_step, C.up(dve_step))
                e.wait_ge(dve_step, C.now(dve_step))
                sk = sink[:, 8 * b + 4 * j:8 * b + 4 * j + 4]
                e.scalar_tensor_tensor(mm_, mx, SCALE, sk, ALU.mult, ALU.max).then_inc(dve_step, C.up(dve_step))
                e.wait_ge(dve_step, C.now(dve_step))
                e.tensor_tensor(sb_, sk, mm_, ALU.subtract)
                e.tensor_scalar(nm, mm_, -1.0, None, ALU.mult).then_inc(maxima_ready, C.up(maxima_ready))

            def sums():
                e.wait_ge(exps_ready, C.next(exps_ready))
                e.tensor_tensor(den, rs, es, ALU.add).then_inc(dve_step, C.up(dve_step))
                e.wait_ge(dve_step, C.now(dve_step))
                e.reciprocal(rinv, den).then_inc(dve_step, C.up(dve_step))

            def output(b, c, j):
                e.wait_ge(full[6], C.next(full[6], 2))
                e.wait_ge(dve_step, C.now(dve_step))
                e.tensor_tensor(
                    otok[:, j * T:(j + 1) * T].rearrange("p (h d) -> p h d", d=HD),
                    ps[:, 6, 0:T].rearrange("p (h d) -> p h d", d=HD),
                    rinv.unsqueeze(2).broadcast_to([P, 4, HD]), ALU.mult).then_inc(free[6], C.up(free[6]))

            def pT_out():
                e.wait_ge(full[7], C.next(full[7]))
                e.tensor_copy(pT[:, 4:8, :], tiles(7)).then_inc(free[7], C.up(free[7]))

            UNITS = [(0, 0), (0, 1), (1, 0), (1, 1)]

            def attention(b, k=8):
                steps = iter(range(k))

                def go(n=1):
                    for _ in range(n):
                        if next(steps, None) is not None:
                            step()

                go(4)
                C.n[full[6]] += 1
                C.n[full[7]] += 1
                go(2)
                maxima(b, *UNITS[0])
                for u, (c, j) in enumerate(UNITS):
                    sums()
                    if u < 3:
                        maxima(b, *UNITS[u + 1])
                    if c:
                        pT_out()
                    if j == 0:
                        go()
                    output(b, c, j)
                    if j:
                        e.wait_ge(full[7], C.next(full[7]))
                        lo(actB[:, 4 * b:4 * b + 4, 1, c * P:(c + 1) * P], tiles(7),
                           actB[:, 4 * b:4 * b + 4, 0, c * P:(c + 1) * P], o_split)
                go(8)

            for i in range(8):
                step()
                if i == 2:
                    e.wait_ge(act_split, C.now(act_split))
                    e.memset(kz[:, :, :].rearrange("p a n -> p (a n)"), 0.0)
            for i in range(8):
                step()
                if i == 0:
                    k_rope()
            C.n[full[6]] += 1
            C.n[full[7]] += 1
            for i in range(8):
                step()
                if i == 0:
                    products()
                    for h in range(NH):
                        e.tensor_copy(vtok[:, h, :], ps[:, 2 + h, :]).then_inc(free[2 + h], C.up(free[2 + h]))
            for b in range(QB):
                C.n[w_used] += 1
                q_rope(2 * (b % 2))
                C.n[w_used] -= 1
                attention(b)
            C.n[free[4]] += 16
            C.n[free[5]] += 8
            e.wait_ge(res_ready, C.next(res_ready))
            for i in range(8, SLAB_CHUNKS):
                step()
                if i % 8 == 0:
                    add_block(i // 8 - 1, True)
            after_products(lambda: add_block(3, True))
            norm(2)
            mlp()
            last_norm()

        @block.gpsimd
        def _(e):
            C = Counts(e, by_dma)

            def select(g):
                e.tensor_copy(sel8[:, :, :], sel2[:, bass.ds(g * GH, GH)].unsqueeze(2)
                                          .broadcast_to([P, GH, P])).then_inc(heads_selected, C.up(heads_selected))

            def rsqrt():
                e.tensor_tensor(rstd, var, mhalf, ALU.pow).then_inc(pool_step, C.up(pool_step))
                e.wait_ge(pool_step, C.now(pool_step))
                e.tensor_tensor(nrt, rstd, rstd, ALU.mult).then_inc(pool_step, C.up(pool_step))
                e.wait_ge(pool_step, C.now(pool_step))
                e.tensor_tensor(nrt, nrt, var, ALU.mult).then_inc(pool_step, C.up(pool_step))
                e.wait_ge(pool_step, C.now(pool_step))
                e.tensor_tensor(nrt, nrt, mhalf, ALU.mult).then_inc(pool_step, C.up(pool_step))
                e.wait_ge(pool_step, C.now(pool_step))
                e.tensor_tensor(nrt, nrt, three_half, ALU.add).then_inc(pool_step, C.up(pool_step))
                e.wait_ge(pool_step, C.now(pool_step))
                return e.tensor_tensor(rstd, rstd, nrt, ALU.mult)

            def group_rstd():
                e.tensor_tensor(var, ss, per_gw, ALU.mult).then_inc(pool_step, C.up(pool_step))
                e.wait_ge(pool_step, C.now(pool_step))
                e.tensor_tensor(var, var, epsilon, ALU.add).then_inc(pool_step, C.up(pool_step))
                e.wait_ge(pool_step, C.now(pool_step))
                rsqrt().then_inc(rstd_ready, C.up(rstd_ready))

            def norm_rstd():
                e.wait_ge(mean_var_ready, C.next(mean_var_ready, 2))
                e.wait_ge(rstd_ready, C.now(rstd_ready))
                e.tensor_tensor(var, mvb[:, :, 1], epsilon, ALU.add).then_inc(pool_step, C.up(pool_step))
                e.wait_ge(pool_step, C.now(pool_step))
                rsqrt().then_inc(pool_step, C.up(pool_step))
                e.wait_ge(pool_step, C.now(pool_step))
                e.tensor_tensor(nmr, mvb[:, :, 0], rstd, ALU.mult).then_inc(pool_step, C.up(pool_step))
                e.wait_ge(pool_step, C.now(pool_step))
                e.tensor_tensor(nmr, nmr, minus_one, ALU.mult).then_inc(rstd_ready, C.up(rstd_ready))

            for x, value in ((mhalf, -0.5), (per_gw, 1.0 / GW), (epsilon, EPS), (three_half, 1.5),
                             (minus_one, -1.0)):
                e.memset(x, value)
            e.wait_ge(selection_ready, C.next(selection_ready))
            e.memset(var, 0.0).then_inc(pool_step, C.up(pool_step))
            select(0)

            def turn(g):
                e.wait_ge(m_ready, C.next(m_ready, 2))
                select(g)
                e.wait_ge(y_squared, C.next(y_squared, 2))
                group_rstd()

            before = dict(C.n)
            turn(1)
            with C.loop(NG - 2, before, 1) as i:
                turn(i + 2)
            e.wait_ge(m_ready, C.next(m_ready, 2))
            e.wait_ge(y_squared, C.next(y_squared, 2))
            group_rstd()

            e.wait_ge(yT_done, C.next(yT_done))
            for h in range(NH):
                e.dma_start(res[:, h, :], t["x"][0, h * P:(h + 1) * P, :]).then_inc(x_again_in, C.up(x_again_in))
            e.wait_ge(x_again_in, C.now(x_again_in))
            e.tensor_scalar(res[:, :, :].rearrange("p c n -> p (c n)"),
                                              res[:, :, :].rearrange("p c n -> p (c n)"), ALPHA, 0.0, ALU.mult, ALU.add).then_inc(
                                                  res_ready, C.up(res_ready))

            def gains(l, scale=True):
                for i, src in enumerate((t["ln_g"], t["ln_b"])):
                    e.dma_start(gb[:, i, :], src[l // 2, l % 2:l % 2 + 1, :].broadcast_to([P, D])).then_inc(
                        gains_in, C.up(gains_in))
                if scale:
                    e.wait_ge(gains_in, C.now(gains_in))
                    e.tensor_scalar(gb[:, :, :].rearrange("p c n -> p (c n)"),
                                         gb[:, :, :].rearrange("p c n -> p (c n)"), ALPHA, 0.0, ALU.mult, ALU.add).then_inc(
                                             pool_step, C.up(pool_step))
                    e.wait_ge(pool_step, C.now(pool_step))

            def residual(splits):
                e.wait_ge(act_split, C.next(act_split, splits))
                for h in range(NH):
                    e.tensor_tensor(res[:, h, :], res[:, h, :], gb[:, 0, :], ALU.mult).then_inc(
                        pool_step, C.up(pool_step))
                    e.wait_ge(pool_step, C.now(pool_step))
                    ins = e.tensor_tensor(res[:, h, :], res[:, h, :], gb[:, 1, :], ALU.add)
                    if h == 0:
                        ins.then_inc(pool_step, C.up(pool_step))
                        e.wait_ge(pool_step, C.now(pool_step))
                ins.then_inc(res_ready, C.up(res_ready))

            norm_rstd()
            e.wait_ge(w_used, C.next(w_used, 1 + NG * GROUP_CHUNKS + 2 * SLAB_CHUNKS))
            gains(0)
            residual(3 * 8)
            e.wait_ge(res_ready, C.now(res_ready))
            gains(1)
            norm_rstd()
            residual(4 * 16 + 8)
            norm_rstd()
            e.wait_ge(o_split, C.next(o_split, 2 * QB))
            gains(2)
            residual(8)
            e.wait_ge(res_ready, C.now(res_ready))
            gains(3, scale=False)
            norm_rstd()


FULLS = {4: 28, 5: 28, 6: 36, 7: 27}
TOTAL = 1 + NG * GROUP_CHUNKS + 2 * SLAB_CHUNKS + 8 * 2 * SLAB_CHUNKS + 16 + 32 + 32


def constants():
    i = np.arange(P)
    c = np.zeros((P, K_END), np.float32)
    c[:, K_ID:K_ID + P] = np.eye(P)
    c[:, K_TRI:K_TRI + P] = i[:, None] <= i[None, :]
    c[:, K_STRI:K_STRI + P] = i[:, None] > i[None, :]
    c[:, K_SMASK:K_SMASK + P] = np.where(i[:, None] <= i[None, :], 0.0, NEG)
    c[:, K_AMASK:K_AMASK + P] = np.where(i[None, :] > i[:, None], 0.0, NEG)
    c[:, K_AMASK + P:K_AMASK + 2 * P] = np.where(i[None, :] <= i[:, None], 0.0, NEG)
    c[:, K_SEL:K_SEL + NHD] = i[:, None] % NHD == np.arange(NHD)[None, :]
    freq = np.float32(10000.0) ** (-np.arange(0, HD, 2, dtype=np.float32) / np.float32(HD))
    ang = np.arange(T, dtype=np.float32)[:, None] * freq[None, :]
    for h in range(NH):
        c[:, K_COS + 32 * h:K_COS + 32 * h + 32] = np.cos(ang[h * P:(h + 1) * P])
        c[:, K_SIN + 32 * h:K_SIN + 32 * h + 32] = np.sin(ang[h * P:(h + 1) * P])
    return c


_INS = ["x", "a_w_in", "a_conv_w", "a_conv_b", "a_dt_bias", "a_A_log", "a_D", "a_norm_w", "a_w_out", "kv_w",
        "b_w_q", "b_sinks", "b_w_o", "mlp_w1", "mlp_w2", "ln_g", "ln_b"]


def kernel(**inputs):
    import concourse.bacc as bacc
    from concourse.bass_utils import run_bass_kernel_spmd

    nc = bacc.Bacc("TRN2", target_bir_lowering=False, num_devices=1)
    arrays, ap = {}, {}
    for name in _INS:
        a = np.ascontiguousarray(inputs[name])
        arrays[f"in_{name}"] = a
        ap[name] = nc.dram_tensor(f"in_{name}", a.shape, mybir.dt.from_np(a.dtype), kind="ExternalInput").ap()
    arrays["in_consts"] = constants()
    consts = nc.dram_tensor("in_consts", (P, K_END), F32, kind="ExternalInput").ap()
    out = nc.dram_tensor("out_0", (1, T, D), F32, kind="ExternalOutput").ap()
    build(nc, {
        "consts": consts, "x": ap["x"], "w_in": ap["a_w_in"][0], "conv_w": ap["a_conv_w"], "conv_b": ap["a_conv_b"],
        "dt_bias": ap["a_dt_bias"], "A_log": ap["a_A_log"], "Dskip": ap["a_D"], "norm_w": ap["a_norm_w"],
        "w_out": ap["a_w_out"][0], "kv_w": ap["kv_w"], "w_q": ap["b_w_q"][0], "sinks": ap["b_sinks"],
        "w_o": ap["b_w_o"][0], "w1": ap["mlp_w1"], "w2": ap["mlp_w2"], "ln_g": ap["ln_g"], "ln_b": ap["ln_b"],
    }, out)
    r = run_bass_kernel_spmd(nc, [arrays], core_ids=[0])
    return r.results[0]["out_0"]
```
